# Optimizing a Trainium2 kernel written in Bass

```python
import jax, jax.numpy as jnp
from jax import lax
import numpy as np

D_MODEL = 1024
BATCH = 1
SEQ = 1024
DEPTH = 1
DEC_BATCH = 8
DEC_SEQ = 4
PAST_LEN = 4096
PAGE_SIZE = 128

HEAD_DIM = 64
N_GROUPS = 3
HEADS_PER_GROUP = 4
N_HEADS = N_GROUPS * HEADS_PER_GROUP
D_ATT = N_HEADS * HEAD_DIM
D_ATT_OUT = HEADS_PER_GROUP * HEAD_DIM
WINDOWS = (128, 512, 2048)
DILATIONS = (1, 4, 16)
C_CONV = D_MODEL
CONV_WIDTH = 31
D_FF = -(-8 * D_MODEL // (3 * 256)) * 256
N_IN = 3 * D_ATT + 2 * C_CONV + 2 * D_MODEL
RMS_EPS = 1e-6
LN_EPS = 1e-5
NEG_INF = -1e30
ATT_SCALE = HEAD_DIM ** -0.5

kernel_name = "dilated_window_conformer_conv_gated_hybrid_step"

def rms_norm(x, w):
    xf = x.astype(jnp.float32)
    y = xf * lax.rsqrt(jnp.mean(xf * xf, axis=-1, keepdims=True) + RMS_EPS)
    return (y * w.astype(jnp.float32)).astype(x.dtype)

def layer_norm(x, w, b):
    xf = x.astype(jnp.float32)
    mu = jnp.mean(xf, axis=-1, keepdims=True)
    xc = xf - mu
    y = xc * lax.rsqrt(jnp.mean(xc * xc, axis=-1, keepdims=True) + LN_EPS)
    return (y * w.astype(jnp.float32) + b.astype(jnp.float32)).astype(x.dtype)

def branch_inputs(x, norm_w, w_in, q_norm_w, k_norm_w):
    xn = rms_norm(x, norm_w)
    z = xn @ w_in
    lead = z.shape[:-1]
    o = 0
    q = z[..., o:o + D_ATT].reshape(*lead, N_GROUPS, HEADS_PER_GROUP, HEAD_DIM); o += D_ATT
    k = z[..., o:o + D_ATT].reshape(*lead, N_GROUPS, HEADS_PER_GROUP, HEAD_DIM); o += D_ATT
    v = z[..., o:o + D_ATT].reshape(*lead, N_GROUPS, HEADS_PER_GROUP, HEAD_DIM); o += D_ATT
    ua = z[..., o:o + C_CONV]; o += C_CONV
    ub = z[..., o:o + C_CONV]; o += C_CONV
    ga = z[..., o:o + D_MODEL]; o += D_MODEL
    gb = z[..., o:o + D_MODEL]
    q = rms_norm(q, q_norm_w)
    k = rms_norm(k, k_norm_w)
    u = ua * jax.nn.sigmoid(ub)
    return q, k, v, u, ga, gb

def window_attn_prompt(q, k, v, window, dil):
    B, T, H, dh = q.shape
    blk = window // dil
    seg = blk * dil
    Tp = -(-T // seg) * seg
    pad = Tp - T
    n = Tp // dil
    nb = n // blk

    def to_blocks(a):
        a = jnp.pad(a, ((0, 0), (0, pad), (0, 0), (0, 0)))
        a = a.reshape(B, n, dil, H, dh).transpose(0, 2, 1, 3, 4)
        return a.reshape(B, dil, nb, blk, H, dh)

    def with_prev(a):
        prev = jnp.pad(a[:, :, :-1], ((0, 0), (0, 0), (1, 0), (0, 0), (0, 0), (0, 0)))
        return jnp.concatenate([prev, a], axis=3)

    qb = to_blocks(q).astype(jnp.float32)
    kk = with_prev(to_blocks(k)).astype(jnp.float32)
    vv = with_prev(to_blocks(v)).astype(jnp.float32)
    s = jnp.einsum('brnqhd,brnkhd->brnhqk', qb, kk) * ATT_SCALE
    qi = jnp.arange(blk)[:, None]
    ki = jnp.arange(2 * blk)[None, :]
    dist = qi + blk - ki
    band = (dist >= 0) & (dist <= blk)
    has_prev = jnp.arange(nb)[:, None, None] > 0
    valid = band[None] & (has_prev | (ki >= blk)[None])
    s = jnp.where(valid[None, None, :, None], s, NEG_INF)
    lse = jax.nn.logsumexp(s, axis=-1)
    p = jnp.exp(s - lse[..., None])
    o = jnp.einsum('brnhqk,brnkhd->brnqhd', p, vv)
    o = o.reshape(B, dil, n, H, dh).transpose(0, 2, 1, 3, 4).reshape(B, Tp, H, dh)[:, :T]
    lse = lse.transpose(0, 1, 2, 4, 3).reshape(B, dil, n, H).transpose(0, 2, 1, 3).reshape(B, Tp, H)[:, :T]
    return o, lse

def window_attn_sample(q, ext_k, ext_v, window, dil):
    S = q.shape[1]
    L = ext_k.shape[1] - S
    J = window // dil
    idx = L + jnp.arange(S)[:, None] - dil * jnp.arange(J + 1)[None, :]
    valid = idx >= 0
    idx = jnp.maximum(idx, 0)
    kg = ext_k[:, idx].astype(jnp.float32)
    vg = ext_v[:, idx].astype(jnp.float32)
    s = jnp.einsum('bshd,bsjhd->bshj', q.astype(jnp.float32), kg) * ATT_SCALE
    s = jnp.where(valid[None, :, None, :], s, NEG_INF)
    lse = jax.nn.logsumexp(s, axis=-1)
    p = jnp.exp(s - lse[..., None])
    o = jnp.einsum('bshj,bsjhd->bshd', p, vg)
    return o, lse

def combine_groups(outs, lses):
    o = jnp.stack(outs, axis=0)
    alpha = jax.nn.softmax(jnp.stack(lses, axis=0), axis=0)
    return jnp.sum(alpha[..., None] * o, axis=0)

def causal_dwconv(u_ext, w, b):
    y = lax.conv_general_dilated(u_ext, w[:, None, :], window_strides=(1,), padding='VALID',
                                 dimension_numbers=('NWC', 'WIO', 'NWC'), feature_group_count=C_CONV)
    return y + b

def merge_and_ffn(x, o_att, c, ga, gb, w_att, conv_ln_w, conv_ln_b, w_conv_out, w_out,
                  norm_ffn_w, w_gate_up, w_down):
    a = o_att.reshape(*o_att.shape[:-2], D_ATT_OUT) @ w_att
    cb = jax.nn.silu(layer_norm(c, conv_ln_w, conv_ln_b)) @ w_conv_out
    h = jax.nn.sigmoid(ga) * a + jax.nn.sigmoid(gb) * cb
    x = x + h @ w_out
    gu = rms_norm(x, norm_ffn_w) @ w_gate_up
    g, up = gu[..., :D_FF], gu[..., D_FF:]
    return x + (jax.nn.silu(g) * up) @ w_down

def setup_inputs(seed: int = 0) -> dict:
    key = jax.random.key(seed)
    ks = jax.random.split(key, 24)
    f32 = jnp.float32
    nrm = lambda k, shape, scale: jax.random.normal(k, shape, f32) * scale
    lens = [min(w, PAST_LEN) for w in WINDOWS]
    return {
        "x_prompt": nrm(ks[0], (BATCH, SEQ, D_MODEL), 1.0),
        "x_sample": nrm(ks[1], (DEC_BATCH, DEC_SEQ, D_MODEL), 1.0),
        "cache_kv_w128": nrm(ks[2], (DEPTH, DEC_BATCH, lens[0], 2, HEADS_PER_GROUP, HEAD_DIM), 1.0),
        "cache_kv_w512": nrm(ks[3], (DEPTH, DEC_BATCH, lens[1], 2, HEADS_PER_GROUP, HEAD_DIM), 1.0),
        "cache_kv_w2048": nrm(ks[4], (DEPTH, DEC_BATCH, lens[2], 2, HEADS_PER_GROUP, HEAD_DIM), 1.0),
        "state_conv": nrm(ks[5], (DEPTH, DEC_BATCH, CONV_WIDTH - 1, C_CONV), 0.5),
        "norm_mix_w": 1.0 + nrm(ks[6], (DEPTH, D_MODEL), 0.02),
        "w_in": nrm(ks[7], (DEPTH, D_MODEL, N_IN), D_MODEL ** -0.5),
        "q_norm_w": 1.0 + nrm(ks[8], (DEPTH, HEAD_DIM), 0.02),
        "k_norm_w": 1.0 + nrm(ks[9], (DEPTH, HEAD_DIM), 0.02),
        "w_att": nrm(ks[10], (DEPTH, D_ATT_OUT, D_MODEL), D_ATT_OUT ** -0.5),
        "conv_w": nrm(ks[11], (DEPTH, CONV_WIDTH, C_CONV), CONV_WIDTH ** -0.5),
        "conv_b": nrm(ks[12], (DEPTH, C_CONV), 0.02),
        "conv_ln_w": 1.0 + nrm(ks[13], (DEPTH, C_CONV), 0.02),
        "conv_ln_b": nrm(ks[14], (DEPTH, C_CONV), 0.02),
        "w_conv_out": nrm(ks[15], (DEPTH, C_CONV, D_MODEL), C_CONV ** -0.5),
        "w_out": nrm(ks[16], (DEPTH, D_MODEL, D_MODEL), D_MODEL ** -0.5),
        "norm_ffn_w": 1.0 + nrm(ks[17], (DEPTH, D_MODEL), 0.02),
        "w_gate_up": nrm(ks[18], (DEPTH, D_MODEL, 2 * D_FF), D_MODEL ** -0.5),
        "w_down": nrm(ks[19], (DEPTH, D_FF, D_MODEL), D_FF ** -0.5),
    }

def reference(x_prompt, x_sample, cache_kv_w128, cache_kv_w512, cache_kv_w2048, state_conv,
              norm_mix_w, w_in, q_norm_w, k_norm_w, w_att, conv_w, conv_b, conv_ln_w, conv_ln_b,
              w_conv_out, w_out, norm_ffn_w, w_gate_up, w_down):
    caches = (cache_kv_w128, cache_kv_w512, cache_kv_w2048)
    xp, xs = x_prompt, x_sample
    p_kv = [[] for _ in WINDOWS]
    s_kv = [[] for _ in WINDOWS]
    p_conv, s_conv = [], []
    for l in range(DEPTH):
        q, k, v, u, ga, gb = branch_inputs(xp, norm_mix_w[l], w_in[l], q_norm_w[l], k_norm_w[l])
        T = xp.shape[1]
        outs, lses = [], []
        for g, (win, dil) in enumerate(zip(WINDOWS, DILATIONS)):
            o, lse = window_attn_prompt(q[:, :, g], k[:, :, g], v[:, :, g], win, dil)
            outs.append(o)
            lses.append(lse)
            lp = min(win, T)
            p_kv[g].append(jnp.stack([k[:, T - lp:, g], v[:, T - lp:, g]], axis=2))
        o_att = combine_groups(outs, lses).astype(xp.dtype)
        u_ext = jnp.pad(u, ((0, 0), (CONV_WIDTH - 1, 0), (0, 0)))
        c = causal_dwconv(u_ext, conv_w[l], conv_b[l])
        p_conv.append(u_ext[:, -(CONV_WIDTH - 1):])
        xp = merge_and_ffn(xp, o_att, c, ga, gb, w_att[l], conv_ln_w[l], conv_ln_b[l], w_conv_out[l],
                           w_out[l], norm_ffn_w[l], w_gate_up[l], w_down[l])

        q, k, v, u, ga, gb = branch_inputs(xs, norm_mix_w[l], w_in[l], q_norm_w[l], k_norm_w[l])
        outs, lses = [], []
        for g, (win, dil) in enumerate(zip(WINDOWS, DILATIONS)):
            new_kv = jnp.stack([k[:, :, g], v[:, :, g]], axis=2)
            ext = jnp.concatenate([caches[g][l].astype(new_kv.dtype), new_kv], axis=1)
            o, lse = window_attn_sample(q[:, :, g], ext[:, :, 0], ext[:, :, 1], win, dil)
            outs.append(o)
            lses.append(lse)
            ln = min(win, ext.shape[1])
            s_kv[g].append(ext[:, ext.shape[1] - ln:])
        o_att = combine_groups(outs, lses).astype(xs.dtype)
        u_ext = jnp.concatenate([state_conv[l].astype(u.dtype), u], axis=1)
        c = causal_dwconv(u_ext, conv_w[l], conv_b[l])
        s_conv.append(u_ext[:, -(CONV_WIDTH - 1):])
        xs = merge_and_ffn(xs, o_att, c, ga, gb, w_att[l], conv_ln_w[l], conv_ln_b[l], w_conv_out[l],
                           w_out[l], norm_ffn_w[l], w_gate_up[l], w_down[l])
    return (xp, xs,
            jnp.stack(p_kv[0]), jnp.stack(s_kv[0]),
            jnp.stack(p_kv[1]), jnp.stack(s_kv[1]),
            jnp.stack(p_kv[2]), jnp.stack(s_kv[2]),
            jnp.stack(p_conv), jnp.stack(s_conv))


_drawn_inputs = setup_inputs


def setup_inputs(seed=0):
    import zlib

    import numpy as np

    out = dict(_drawn_inputs(seed))
    spreads = {}
    factors = {'q_norm_w': 8.0,
     'k_norm_w': 3.685,
     'conv_b': 4.033,
     'conv_ln_w': 6.61,
     'conv_ln_b': 8.0,
     'norm_ffn_w': 4.034}
    for name, (base, spread) in spreads.items():
        noise = np.random.default_rng([zlib.crc32(name.encode()), seed]).standard_normal(out[name].shape)
        drawn = base * np.exp(spread * noise) if base else spread * noise
        out[name] = __import__('jax').numpy.asarray(drawn.astype(out[name].dtype))
    for name, factor in factors.items():
        out[name] = (out[name] * factor).astype(out[name].dtype)
    return out
```

```python
from contextlib import ExitStack

import concourse.bass as bass
from concourse import mybir

F32 = mybir.dt.float32
F32R = mybir.dt.float32r
ALU = mybir.AluOpType
ACT = mybir.ActivationFunctionType
AX_X = mybir.AxisListType.X
ds = bass.ds

P = 128
D = 1024
SEQ = 1024
DEC_B, DEC_S = 8, 4
NS = DEC_B * DEC_S
T = SEQ + NS
NCH = 3
CH = T // NCH
PC2 = SEQ - 2 * CH
KT = D // P
HD = 64
NG, NH = 3, 4
GW = NH * HD
DATT = NG * GW
WIN = (128, 512, 2048)
DIL = (1, 4, 16)
CW = 31
HIST = CW - 1
SEG = HIST + DEC_S
ULEN = HIST + SEQ + DEC_B * SEG
DFF = 2816
FT = DFF // P
SCALE = HD ** -0.5
RMS_EPS, LN_EPS = 1e-6, 1e-5
NEG = -1e30

OFF_Q = 0
OFF_UA = 3 * DATT
OFF_UB = OFF_UA + D
OFF_GA = OFF_UB + D
OFF_GB = OFF_GA + D

GLU0 = 0
QKV0 = GLU0 + 2 * KT
GATE0 = QKV0 + 6 * NG
ATT0 = GATE0 + 2 * KT
CO0 = ATT0 + 2
OUT0 = CO0 + KT
FFN0 = OUT0 + KT
NIT = FT // 2
NJOBS = FFN0 + 6 * NIT
Z_ATT0 = ATT0
Z_CO0 = Z_ATT0 + KT
Z_OUT0 = Z_CO0 + KT
Z_FFN0 = Z_OUT0 + KT
FREED_BY_ACT = KT

TAPS_GLU = 13
TAPS_QKV = 9
V_B, V_LW, V_LB, V_NF = CW, CW + 1, CW + 2, CW + 3
NVEC = CW + 4
SW = 256 + 8


def build(nc, a):
    ctx = ExitStack()
    base = (nc.sbuf_base + 63) // 64 * 64
    cursor = [base]

    def at(name, shape, dt, offset):
        return nc.alloc_sbuf_tensor_at(name, shape, dt, offset=offset)

    def perm(name, shape, dt=F32):
        n = 4
        for s in shape[1:]:
            n *= s
        t = at(name, shape, dt, cursor[0])
        cursor[0] += (n + 31) // 32 * 32
        return t

    ident = perm("ident", [P, P])
    headmean = perm("headmean", [P, P])
    allmean = perm("allmean", [P, P])
    band = perm("band", [P, 2 * P])
    pair = perm("pair", [P, P])
    smask = perm("smask", [P, NG, 2 * P])
    vec = perm("vec", [P, KT, NVEC])
    qkw = perm("qkw", [P, 2])
    eps = perm("eps", [P, 2])
    ss = perm("ss", [P, 16])
    rs9 = perm("rs9", [P, 16])
    raw = [perm(f"raw{i}", [P, 1024]) for i in range(2)]
    whi = [perm(f"whi{i}", [P, 1024], F32R) for i in range(2)]
    wlo = [perm(f"wlo{i}", [P, 1024], F32R) for i in range(2)]
    R0 = cursor[0]
    REG = KT * T * 4
    S1, S2, S3, S4, S5 = (R0 + i * REG for i in range(5))

    xhi = at("xhi", [P, KT, T], F32R, S1)
    xlo = at("xlo", [P, KT, T], F32R, S2)
    conv = at("conv", [P, KT, T], F32, S3)
    misc = S4
    zt = [at(f"zt{i}", [P, T], F32, misc + i * T * 4) for i in range(2)]
    sg = at("sg", [P, T], F32, misc + 2 * T * 4)
    sqb = at("sqb", [P, T], F32, misc + 3 * T * 4)
    rsb = at("rsb", [P, T], F32, misc + 4 * T * 4)
    U0 = misc + 5 * T * 4
    u = at("u", [P, KT, ULEN], F32, U0)
    utail = at("utail", [P, KT, NS], F32, misc + 2 * T * 4)
    urow = at("urow", [HIST, D], F32, U0 + KT * ULEN * 4 + 4096)
    urows = at("urows", [NS, D], F32, U0 + KT * ULEN * 4 + 8192)
    sprod = at("sprod", [P, DEC_B, DEC_S, CW], F32, U0 + KT * ULEN * 4)
    xtok = at("xtok", [P, KT + 1, D], F32, S3)
    wb = at("wb", [P, D], F32, S3 + 9 * D * 4)
    vrow = at("vrow", [P, D], F32, S3 + 10 * D * 4)
    srow = at("srow", [P, 2, D], F32, S3 + 11 * D * 4)
    assert S3 + 13 * D * 4 <= U0
    junk = at("junk", [P, D], F32, U0 + KT * ULEN * 4)

    qk = at("qk", [P, NG, 4, T], F32, S1)
    vt = [at(f"vt{i}", [P, 2, T], F32, S1 + (12 + 2 * i) * T * 4) for i in range(2)]
    othi = at("othi", [P, 2, T], F32R, S1 + 12 * T * 4)
    otlo = at("otlo", [P, 2, T], F32R, S1 + 14 * T * 4)
    o12 = at("o12", [P, 2, KT, SW], F32, S1)
    cur2 = [S4]

    def reg(name, shape, dt=F32):
        n = 4
        for x in shape[1:]:
            n *= x
        t = at(name, shape, dt, cur2[0])
        cur2[0] += (n + 31) // 32 * 32
        return t

    kv = reg("kv", [P, NG, KT, 2, GW])
    pb = reg("pb", [P, 2, NH, 2 * P])
    pt = reg("pt", [P, 2, 2 * NH, P])
    o0 = reg("o0", [P, KT, SW])
    ob = reg("ob", [P, 4, SW])
    nmx = reg("nmx", [P, 2, NH])
    srows = at("srows", [P, NG, 3, GW], F32, S4 + NG * KT * 2 * GW * 4)
    lsq = at("lsq", [P, 2, T], F32, S4 + 0)
    lrs = at("lrs", [P, T], F32, S4 + 2 * T * 4)
    cur2 = [S4]
    kc = [reg(f"kc{i}", [P, DEC_S, GW]) for i in range(4)]
    qb = [reg(f"qb{i}", [P, DEC_S, GW]) for i in range(2)]
    prod = [reg(f"prod{i}", [P, DEC_S, GW]) for i in range(2)]
    sc = reg("sc", [P, NG, P])
    prow = reg("prow", [P, NG, 2 * P])
    ptr = reg("ptr", [P, NG, 2, P])
    rowqk = reg("rowqk", [P, NG, 2, HD])
    rowv = reg("rowv", [P, NG, 2, HD])
    rowt = reg("rowt", [P, NG, 2, P])
    sst = reg("sst", [P, 4])
    assert cur2[0] <= S4 + NG * KT * 2 * GW * 4
    cw = [at(f"cw{i}", [P, KT, NH], F32, S4 + i * 128) for i in range(10)]
    ctmp = at("ctmp", [P, KT, GW], F32, S4 + 2048)
    shi = at("shi", [P, KT, T], F32R, S1)
    slo = at("slo", [P, KT, T], F32R, S3)
    ha = at("ha", [P, KT, T], F32, S4)
    hhi = at("hhi", [P, KT, T], F32R, S4)
    hlo = at("hlo", [P, KT, T], F32R, S2)
    sgs = [at(f"sgs{i}", [P, T], F32, S5 + i * T * 4) for i in range(2)]
    ht = [at(f"ht{i}", [P, T], F32, S5 + (2 + i) * T * 4) for i in range(2)]
    x1 = at("x1", [P, KT, T], F32, S1)
    xj = [at(f"xj{i}", [P, KT + 1, P], F32, S5 + 4 * T * 4 + i * 4608) for i in range(2)]
    xtj = at("xtj", [P, T], F32, S5 + 4 * T * 4 + 9216)
    sqs = at("sqs", [P, T], F32, S5 + 5 * T * 4 + 9216)
    sqj = at("sqj", [P, T], F32, S5 + 6 * T * 4 + 9216)
    nhi = at("nhi", [P, KT, T], F32R, S3)
    nlo = at("nlo", [P, KT, T], F32R, S2)
    achi = [at(f"achi{i}", [P, 2, T], F32R, S4 + i * 2 * T * 4) for i in range(2)]
    aclo = [at(f"aclo{i}", [P, 2, T], F32R, S4 + (4 + 2 * i) * T * 4) for i in range(2)]
    sil = [at(f"sil{i}", [P, T], F32, S5 + i * T * 4) for i in range(2)]
    ytok = [at(f"ytok{i}", [P, D], F32, S5 + i * D * 4) for i in range(4)]

    ps = ctx.enter_context(nc.psum_tensor("ps", [P, 8, 512], F32))

    def sem(name):
        return ctx.enter_context(nc.semaphore(name))

    s_const = sem("s_const")
    s_ut, s_urow = sem("s_ut"), sem("s_urow")
    s_x = [sem(f"s_x{t}") for t in range(KT + 1)]
    s_ss, s_rs, s_xs, s_tr, s_ahi, s_alo = (sem(n) for n in ("s_ss", "s_rs", "s_xs", "s_tr", "s_ahi", "s_alo"))
    s_vt, s_vec, s_stt, s_stu, s_pad = (sem(n) for n in ("s_vt", "s_vec", "s_stt", "s_stu", "s_pad"))
    s_raw = [sem(f"s_raw{i}") for i in range(2)]
    s_hi, s_lo, s_pe = sem("s_hi"), sem("s_lo"), sem("s_pe")
    s_z = [sem(f"s_z{i}") for i in range(2)]
    s_zfd = [sem(f"s_zfd{i}") for i in range(2)]
    s_zfa = [sem(f"s_zfa{i}") for i in range(2)]
    s_sig, s_conv = sem("s_sig"), sem("s_conv")
    s_sq, s_ssr, s_sqrt = sem("s_sq"), sem("s_ssr"), sem("s_sqrt")
    s_ztd, s_zta = sem("s_ztd"), sem("s_zta")
    s_zst = [sem(f"s_zst{i}") for i in range(2)]
    s_utail, s_pexp0, s_fin = sem("s_utail"), sem("s_pexp0"), sem("s_fin")
    move_rows = []
    s_ln = {n: sem(f"ln_{n}") for n in ("mean", "cen", "sq", "var", "root", "norm", "act")}
    s_kvt, s_kva, s_kvd, s_vfree, s_srows = (sem(n) for n in ("s_kvt", "s_kva", "s_kvd", "s_vfree", "s_srows"))
    s_vin = [sem(f"s_vin{i}") for i in range(2)]
    s_qk = [sem(f"s_qk{g}") for g in range(NG)]
    s_S, s_max, s_P, s_PT, s_pta, s_ptd, s_O, s_Oe = (sem(n) for n in ("s_S", "s_max", "s_P", "s_PT", "s_pta", "s_ptd", "s_O", "s_Oe"))
    s_ost = [sem(f"s_ost{i}") for i in range(4)]
    s_kc = [sem(f"s_kc{i}") for i in range(4)]
    s_qb = [sem(f"s_qb{i}") for i in range(2)]
    s_prod, s_sc, s_row, s_rowT, s_rowt, s_snew, s_prow, s_pexp, s_ppT, s_ptr, s_pv, s_kcf = (
        sem(n) for n in ("s_prod", "s_sc", "s_row", "s_rowT", "s_rowt", "s_snew", "s_prow", "s_pexp", "s_ppT", "s_ptr", "s_pv", "s_kcf"))
    s_o12, s_cd, s_cw, s_comb, s_oT, s_oTh, s_oTl = (sem(n) for n in ("s_o12", "s_cd", "s_cw", "s_comb", "s_oT", "s_oTh", "s_oTl"))
    s_shi, s_slo = sem("s_shi"), sem("s_slo")
    s_sgs = [sem(f"s_sgs{i}") for i in range(2)]
    s_ht, s_hhi, s_hlo = sem("s_ht"), sem("s_hhi"), sem("s_hlo")
    s_xj = [sem(f"s_xj{i}") for i in range(2)]
    s_xT, s_xte, s_x1, s_sqj, s_sqs, s_r2, s_r2s, s_n, s_nhi, s_nlo = (
        sem(n) for n in ("s_xT", "s_xte", "s_x1c", "s_sqj", "s_sqs", "s_r2", "s_r2s", "s_n", "s_nhi", "s_nlo"))
    s_sil, s_gt, s_ahi2, s_alo2 = sem("s_sil"), sem("s_gt"), sem("s_ahi2"), sem("s_alo2")
    s_yT, s_yea, s_yed = sem("s_yT"), sem("s_yea"), sem("s_yed")
    s_yst = [sem(f"s_yst{i}") for i in range(4)]
    s_out, s_cache = sem("s_out"), sem("s_cache")

    def job_use(n):
        if n < ATT0:
            return n
        if n < CO0:
            return Z_ATT0 + 4 * (n - ATT0) + 3
        if n < FFN0 + 4:
            return Z_CO0 + n - CO0
        if n >= NJOBS - 2:
            return Z_FFN0 + 12 * NIT - (8 if n == NJOBS - 2 else 4) + 3
        k, i = (n - FFN0 - 4) % 6, (n - FFN0 - 4) // 6
        return Z_FFN0 + 4 + 12 * i + (0, 1, 2, 3, 7, 11)[k]

    def finished(eng, n):
        use = job_use(n)
        eng.wait_ge(s_z[use % 2], NCH * (use // 2 + 1))

    ATT_BLOCKS = [(g, b) for g in range(NG) for b in range(KT)]
    NB = len(ATT_BLOCKS)

    def two_key_blocks(g, b):
        return (g == 0 and b > 0) or (g == 1 and b % 2 == 1)

    KV_MOVES = []
    for g in range(NG):
        ks = [(KT - 1, 1, 1)] if g == 0 else [(1, 2, 2), (5, 2, 2)] if g == 1 else [(2 * b, 1, 2) for b in range(4)]
        KV_MOVES.append([(0,) + x for x in ks] + [(1, 2 * b, 1, 2) for b in range(4)])
    MOVES = [(g, mv) for g in range(NG) for mv in KV_MOVES[g] + [("s", 0), ("s", 1)]]


    w_in = a["w_in"][0]
    scr_z = a["scr_z"]

    def win_cols(c0):
        return w_in[:, ds(c0, P)].rearrange("(k p) f -> p k f", p=P)

    scr_q, scr_o = a["scr_q"], a["scr_o"]
    NOUT_C = 1 + DEC_B + 1 + 4 + 16 + NG * DEC_B
    NCACHE = 2 * DEC_B + 4 * DEC_B + 1

    def tile_cols(w, c0):
        return w[0][:, ds(c0, P)].rearrange("(k p) f -> p k f", p=P)

    def att_half(h):
        return a["w_att"][0][:, h * 512:(h + 1) * 512].rearrange("(k p) f -> p k f", p=P)

    def down_half(i, h):
        return a["w_down"][0][ds(i * (2 * P), 2 * P), h * 512:(h + 1) * 512].rearrange("(k p) f -> p k f", p=P)

    def z(s, c):
        return ps[:, 3 * s + c, 0:CH]

    def cols(c):
        return slice(c * CH, (c + 1) * CH)

    def permuted(g, dst, src, c):
        d = DIL[g]
        n = CH if c < 2 else PC2
        if d == 1:
            return [(dst[:, cols(c)], src)]
        to = dst[:, 0:SEQ].rearrange("p (r i) -> p i r", r=d)[:, c * CH // d:(c * CH + n) // d, :]
        pairs = [(to, src[:, 0:n].rearrange("p (i r) -> p i r", r=d))]
        if c == 2:
            pairs.append((dst[:, SEQ:T], src[:, PC2:CH]))
        return pairs

    block = ctx.enter_context(nc.Block())

    @block.sync
    def _(sp):
        def load(slot, src, wait_lo=None):
            if wait_lo is not None:
                sp.wait_ge(s_lo, wait_lo)
            k = src.shape[1]
            sp.dma_start(raw[slot][:, :].rearrange("p (k f) -> p k f", k=k), src).then_inc(s_raw[slot], 16)

        for t in range(KT):
            sp.dma_start(xtok[:, t, :], a["x_prompt"][0, t * P:(t + 1) * P, :]).then_inc(s_x[t], 16)
            if t == 0:
                sp.dma_start(wb[:, :], a["norm_mix_w"].partition_broadcast(P).rearrange("q a d -> q (a d)")).then_inc(s_const, 16)
                sp.dma_start(ident[:, :], a["c_ident"]).then_inc(s_const, 16)
        sp.dma_start(xtok[0:NS, KT, :], a["x_sample"].rearrange("b s d -> (b s) d")).then_inc(s_x[KT], 16)
        sp.dma_start(vrow[0:CW, :], a["conv_w"][0]).then_inc(s_const, 16)
        for i, n in enumerate(("conv_b", "conv_ln_w", "conv_ln_b", "norm_ffn_w")):
            sp.dma_start(vrow[CW + i:CW + i + 1, :], a[n]).then_inc(s_const, 16)
        for h in range(2):
            sp.dma_start(srow[0:4 * HIST, h, :], a["state_conv"][0, 4 * h:4 * h + 4].rearrange("b r c -> (b r) c")).then_inc(s_const, 16)
        for t_, n_ in ((headmean, "c_headmean"), (allmean, "c_allmean"), (band, "c_band"), (pair, "c_pair")):
            sp.dma_start(t_[:, :], a[n_]).then_inc(s_const, 16)
        sp.dma_start(smask[:, :, :], a["c_smask"]).then_inc(s_const, 16)
        load(0, win_cols(OFF_UA))
        load(1, win_cols(OFF_UB))
        with nc.allow_non_contiguous_dma(reason="128 weights"):
            for i, n in enumerate(("q_norm_w", "k_norm_w")):
                for h in range(2):
                    sp.dma_start(qkw[HD * h:HD * h + HD, i:i + 1], a[n].rearrange("a d -> d a")).then_inc(s_const, 16)
        with sp.Fori(1, KT) as j:
            load(0, win_cols(j * P + OFF_UA), 2 * j - 1)
            load(1, win_cols(j * P + OFF_UB), 2 * j)

        def store(m):
            n = m - QKV0
            if n < 6 * NG:
                sp.wait_ge(s_ztd, NCH * (n + 1))
            else:
                sp.wait_ge(s_zta, NCH * (n - 6 * NG + 1))
            sp.dma_start(scr_z[n], zt[m % 2][:, :]).then_inc(s_zst[m % 2], 16)

        for g in range(NG):
            for i in range(6):
                m = QKV0 + 6 * g + i
                load(m % 2, win_cols(OFF_Q + (i // 2) * DATT + g * GW + (i % 2) * P), m - 1)
                if m - 3 >= QKV0:
                    store(m - 3)
        for j in range(KT):
            for i in range(2):
                m = GATE0 + 2 * j + i
                load(i, win_cols((OFF_GA, OFF_GB)[i] + j * P), m - 1)
                store(m - 3)
        load(0, att_half(0), ATT0 - 1)
        store(ATT0 - 3)
        load(1, att_half(1), ATT0)
        store(ATT0 - 2)
        store(ATT0 - 1)
        for i in range(2):
            sp.wait_ge(s_zst[i], 16 * (ATT0 - QKV0) // 2)
            sp.wait_ge(s_z[i], NCH * (ATT0 // 2))

        def load_v(g):
            if g == 2:
                sp.wait_ge(s_vfree, 1)
            sp.dma_start(vt[g % 2][:, :, :], scr_z[6 * g + 4:6 * g + 6].rearrange("n p t -> p n t")).then_inc(s_vin[g % 2], 16)

        for g in range(NG):
            sp.dma_start(qk[:, g, :, :], scr_z[6 * g:6 * g + 4].rearrange("n p t -> p n t")).then_inc(s_qk[g], 16)
            load_v(g)
        sp.wait_ge(s_urow, 1)
        sp.dma_start(a["conv_prompt"][0, 0], urow[0:HIST, :]).then_inc(s_out, 16)
        sp.wait_ge(s_urow, 2)
        for b in range(DEC_B):
            sp.dma_start(a["conv_sample"][0, b, HIST - DEC_S:HIST, :], urows[DEC_S * b:DEC_S * b + DEC_S, :]).then_inc(s_out, 16)
        for g in range(NG):
            n = len(KV_MOVES[g]) + 2
            tot = sum(len(KV_MOVES[x]) + 2 for x in range(g)) + n
            sp.wait_ge(s_kva, (tot + 1) // 2)
            sp.wait_ge(s_kvd, tot // 2)
            rows = kv[:, g].rearrange("p b k d -> p b (k d)")
            out = a[f"kv_prompt{g}"][0, 0].rearrange("t k h d -> t (k h d)")
            if g == 0:
                sp.dma_start(out, rows[:, KT - 1, :]).then_inc(s_out, 16)
            elif g == 1:
                for r in range(4):
                    sp.dma_start(out[r:WIN[1]:4, :], rows[:, 2 * r + 1, :]).then_inc(s_out, 16)
            else:
                for r in range(16):
                    sp.dma_start(out[r:SEQ:16, :], rows[HD * (r % 2):HD * (r % 2) + HD, r // 2, :]).then_inc(s_out, 16)
            for b in range(DEC_B):
                sp.dma_start(a[f"kv_sample{g}"][0, b, WIN[g] - DEC_S:WIN[g]].rearrange("t k h d -> t (k h d)"),
                             srows[DEC_S * b:DEC_S * b + DEC_S, g, 1:3, :].rearrange("p k d -> p (k d)")).then_inc(s_out, 16)
            sp.dma_start(scr_q[g].rearrange("k r d -> r k d"), srows[0:NS, g, :, :]).then_inc(s_srows, 16)
        for n, (g, b) in enumerate(ATT_BLOCKS):
            if g == 0:
                continue
            sp.wait_ge(s_Oe, n + 1)
            if g == 1:
                r0 = b // 2 + 512 * (b % 2)
                sp.dma_start(scr_o[0, r0:r0 + 509:4, :], ob[:, n % 4, :]).then_inc(s_ost[n % 4], 16)
            else:
                for h in range(2):
                    sp.dma_start(scr_o[1, 2 * b + h:SEQ:16, :], ob[HD * h:HD * h + HD, n % 4, :]).then_inc(s_ost[n % 4], 16)
        for i in range(4):
            sp.wait_ge(s_ost[i], 16 * 2 + 32 * 2)
        sp.wait_ge(s_S, NB)
        for x in range(2):
            sp.dma_start(o12[:, x], scr_o[x].rearrange("(t p) c -> p t c", p=P)).then_inc(s_o12, 16)
        sp.wait_ge(s_O, NB)
        sp.wait_ge(s_srows, 16 * NG)
        sp.wait_ge(s_out, 16 * NOUT_C)
        for g in range(NG):
            rows = scr_q[g].rearrange("k r (h d) -> k (r h) d", h=NH)
            for k in range(2):
                sp.dma_start(rowqk[:, g, k, :], rows[k]).then_inc(s_row, 16)
                sp.dma_start(rowv[:, g, k, :], rows[2]).then_inc(s_row, 16)

        def cache_tile(n, kind, g, b):
            c = a[("cache_kv_w128", "cache_kv_w512", "cache_kv_w2048")[g]][0, b, :, kind].rearrange("t h d -> t (h d)")
            if n >= 4:
                if n - 4 < NG * DEC_B:
                    sp.wait_ge(s_prod, n - 4 + 1)
                else:
                    sp.wait_ge(s_kcf, n - 4 - NG * DEC_B + 1)
            if g == 0:
                sp.dma_start(kc[n % 4][:, 0, :], c).then_inc(s_kc[n % 4], 16)
            else:
                sp.dma_start(kc[n % 4][:, :, :], c.rearrange("(i r) d -> i r d", r=DIL[g])[:, 0:DEC_S, :]).then_inc(s_kc[n % 4], 16)

        for n in range(NG * DEC_B):
            g, b = n // DEC_B, n % DEC_B
            cache_tile(n, 0, g, b)
            if n >= 2:
                sp.wait_ge(s_prod, n - 1)
            sp.dma_start(qb[n % 2][:, :, :].rearrange("p s d -> p (s d)"),
                         scr_q[g, 0, DEC_S * b:DEC_S * b + DEC_S, :].rearrange("r d -> (r d)").partition_broadcast(P)).then_inc(s_qb[n % 2], 16)
        for n in range(NG * DEC_B):
            cache_tile(NG * DEC_B + n, 1, n // DEC_B, n % DEC_B)
        def gate_load(n):
            if n >= 2:
                if n - 2 < KT:
                    sp.wait_ge(s_zfd[(n - 2) % 2], NCH * (GATE0 // 2 + (n - 2) // 2 + 1))
                else:
                    sp.wait_ge(s_zfd[(n - 2) % 2], NCH * (GATE0 // 2 + (n - 2) // 2 + 1))
            else:
                sp.wait_ge(s_oTl, 6)
            src = 6 * NG + (2 * n if n < KT else 2 * (n - KT) + 1)
            sp.dma_start(sgs[n % 2][:, :], scr_z[src]).then_inc(s_sgs[n % 2], 16)

        def xj_load(j):
            if j >= 2:
                sp.wait_ge(s_xT, 3 * (j - 1))
            sp.dma_start(xj[j % 2][:, 0:KT, :], a["x_prompt"][0, :, j * P:(j + 1) * P].rearrange("(t p) f -> p t f", p=P)).then_inc(s_xj[j % 2], 16)
            sp.dma_start(xj[j % 2][0:NS, KT, :], a["x_sample"].rearrange("b s d -> (b s) d")[:, j * P:(j + 1) * P]).then_inc(s_xj[j % 2], 16)

        gate_load(0)
        gate_load(1)
        load(0, tile_cols(a["w_conv_out"], 0), CO0 - 1)
        load(1, tile_cols(a["w_conv_out"], P), CO0)
        for n in range(2, KT):
            gate_load(n)
        for j in range(KT):
            gate_load(KT + j)
            m = CO0 + j + 2
            load(m % 2, tile_cols(a["w_conv_out"], (j + 2) * P) if j + 2 < KT else tile_cols(a["w_out"], (j + 2 - KT) * P), m - 1)
        xj_load(0)
        xj_load(1)
        gu = a["w_gate_up"][0]
        for j in range(KT):
            m = OUT0 + j + 2
            src = tile_cols(a["w_out"], (j + 2) * P) if j + 2 < KT else tile_cols(a["w_gate_up"], 0 if j + 2 == KT else DFF)
            load(m % 2, src, m - 1)
            if j + 2 < KT:
                xj_load(j + 2)
        load(0, tile_cols(a["w_gate_up"], P), FFN0 + 1)
        load(1, tile_cols(a["w_gate_up"], DFF + P), FFN0 + 2)
        with sp.Fori(0, NIT - 1) as i:
            for k in range(6):
                c0 = i * (2 * P) + (0, DFF, P, DFF + P, 0, 0)[k] + 2 * P
                src = tile_cols(a["w_gate_up"], c0) if k < 4 else down_half(i, k - 4)
                load(k % 2, src, 6 * i + (FFN0 + 4 + k - 1))
        for k in range(2):
            load(k, down_half(NIT - 1, k), NJOBS - 3 + k)
        for t in range(KT + 1):
            n = P if t < KT else NS
            sp.wait_ge(s_yea, t + 1)
            sp.wait_ge(s_yed, t + 1)
            dst = a["y_prompt"][0, t * P:(t + 1) * P, :] if t < KT else a["y_sample"].rearrange("b s d -> (b s) d")
            sp.dma_start(dst, ytok[t % 4][0:n, :]).then_inc(s_yst[t % 4], 16)
        for i in range(4):
            sp.wait_ge(s_yst[i], 16 * ((KT + 1 + 3 - i) // 4))
        sp.wait_ge(s_out, 16 * NOUT_C)
        sp.wait_ge(s_cache, 16 * NCACHE)

    @block.gpsimd
    def _(pool):
        for g, name in enumerate(("cache_kv_w128", "cache_kv_w512", "cache_kv_w2048")):
            keep = WIN[g] - DEC_S
            for b in range(DEC_B):
                src = a[name][0, b, DEC_S:WIN[g]].rearrange("t k h d -> t (k h d)")
                dst = a[f"kv_sample{g}"][0, b, 0:keep].rearrange("t k h d -> t (k h d)")
                if g == 2:
                    for q in range(4):
                        pool.wait_ge(s_lo, FFN0 + 1 + (4 * b + q) * 2)
                        r = slice(q * keep // 4, (q + 1) * keep // 4)
                        pool.dma_start(dst[r, :], src[r, :]).then_inc(s_cache, 16)
                else:
                    pool.wait_ge(s_lo, (4 if g else 2) * b + 3)
                    pool.dma_start(dst, src).then_inc(s_cache, 16)
        pool.dma_start(a["conv_sample"][0, :, 0:HIST - DEC_S, :], a["state_conv"][0, :, DEC_S:HIST, :]).then_inc(s_cache, 16)

    NC0 = 2 + 5 + 2 + 1 + 4 + 4

    @block.tensor
    def _(pe):
        def split_products(out, w, k, rhs_hi, rhs_lo, first, last):
            wh, wl = w
            pe_mm = nc.tensor.matmul
            pe_mm(out, wh, rhs_hi, start=first, stop=False)
            pe_mm(out, wh, rhs_lo, start=False, stop=False)
            return pe_mm(out, wl, rhs_hi, start=False, stop=last)

        def wk(slot, k):
            return (whi[slot][:, k * P:(k + 1) * P], wlo[slot][:, k * P:(k + 1) * P])

        pe.wait_ge(s_const, 16 * NC0)
        for t in range(KT + 1):
            n = P if t < KT else NS
            pe.wait_ge(s_xs, t + 1)
            for h in range(2):
                grp = 2 * t + h
                if grp >= 4:
                    pe.wait_ge(s_alo, grp - 3)
                for k in range(4):
                    mm = nc.tensor.transpose(ps[:, grp % 4, k * n:(k + 1) * n],
                                             xtok[0:n, t, (4 * h + k) * P:(4 * h + k + 1) * P], ident[0:n, 0:n])
                mm.then_inc(s_tr, 1)
        for k in range(KT):
            mm = nc.tensor.transpose(ps[:, 4, k * NVEC:(k + 1) * NVEC], vrow[0:NVEC, k * P:(k + 1) * P], ident[0:NVEC, 0:NVEC])
        mm.then_inc(s_vt, 1)
        hn = 4 * HIST
        for k in range(KT):
            if k >= 2:
                pe.wait_ge(s_stu, k - 1)
            for h in range(2):
                mm = nc.tensor.transpose(ps[:, 5 + k % 2, h * hn:(h + 1) * hn], srow[0:hn, h, k * P:(k + 1) * P], ident[0:hn, 0:hn])
            mm.then_inc(s_stt, 1)

        def tile_job(slot, n, rhs_hi, rhs_lo, free=None, after=None):
            pe.wait_ge(s_lo, n + 1)
            for c in range(NCH):
                if free:
                    pe.wait_ge(free[0][slot], free[1] + c)
                for k in range(KT):
                    mm = split_products(z(slot, c), wk(slot, k), k, rhs_hi[:, k, cols(c)], rhs_lo[:, k, cols(c)], k == 0, k == KT - 1)
                mm.then_inc(s_z[slot], 1)
                if after:
                    after(c)

        pe.wait_ge(s_alo, 2 * (KT + 1))
        pe.wait_ge(s_stu, KT)
        for s in range(2):
            tile_job(s, s, xhi, xlo)
        with pe.Fori(1, KT) as j:
            for s in range(2):
                tile_job(s, 2 * j + s, xhi, xlo, (s_zfd, NCH * j - (NCH - 1)))
        with pe.Fori(0, NG) as g:
            for i in range(6):
                def mean_squares(c, i=i):
                    q = NCH * (i - 1) + c
                    pe.wait_ge(s_sq, 12 * g + (q + 1))
                    if q >= 2:
                        pe.wait_ge(s_sqrt, 12 * g + (q - 1))
                    nc.tensor.matmul(ps[:, 6 + q % 2, 0:CH], headmean[:, :], sqb[:, cols(c)], start=True, stop=True).then_inc(s_ssr, 1)
                tile_job(i % 2, 6 * g + (QKV0 + i), xhi, xlo, (s_zfd, 3 * NCH * g + (NCH * (QKV0 // 2 + i // 2 - 1) + 1)),
                         after=mean_squares if 1 <= i <= 4 else None)
        for s in range(2):
            tile_job(s, GATE0 + s, xhi, xlo, (s_zfd, NCH * (GATE0 // 2 - 1) + 1))
        with pe.Fori(1, KT) as j:
            for s in range(2):
                tile_job(s, 2 * j + (GATE0 + s), xhi, xlo, (s_zfa, NCH * j - (NCH - 1)))

        for s in range(2):
            pe.wait_ge(s_zfa[s], NCH * KT)
        for x in range(2):
            n = HIST if x == 0 else NS
            for k in range(KT):
                if x == 0:
                    src = u[:, k, SEQ:SEQ + HIST]
                else:
                    src = utail[:, k, :]
                    pe.wait_ge(s_utail, 1)
                mm = nc.tensor.transpose(ps[0:n, 2 * x + k // 4, (k % 4) * P:(k % 4 + 1) * P], src, ident[:, :])
            mm.then_inc(s_ut, 1)
        pe.wait_ge(s_conv, 1)
        for c in range(NCH):
            for k in range(KT):
                mm = nc.tensor.matmul(ps[:, 4 + c, 0:CH], allmean[:, :], conv[:, k, cols(c)], start=k == 0, stop=k == KT - 1)
            mm.then_inc(s_ln["mean"], 1)
        pe.wait_ge(s_ln["cen"], KT)
        for k in range(KT):
            pe.wait_ge(s_ln["sq"], k + 1)
            for c in range(NCH):
                mm = nc.tensor.matmul(ps[:, 4 + c, 0:CH], allmean[:, :], lsq[:, k % 2, cols(c)], start=k == 0, stop=k == KT - 1)
            mm.then_inc(s_ln["var"], 1)

        for n, (g, mv) in enumerate(MOVES):
            if n >= 8:
                pe.wait_ge((s_kva, s_kvd)[n % 2], (n - 8) // 2 + 1)
            elif n >= 4:
                pe.wait_ge(s_ln["root"], NCH)
            else:
                pe.wait_ge(s_urow, 2)
            pe.wait_ge(s_qk[g], 16)
            pe.wait_ge(s_vin[g % 2], 16 * (g // 2 + 1))
            if mv[0] == "s":
                for x in range(4 if mv[1] == 0 else 2):
                    src = qk[:, g, x, SEQ:T] if mv[1] == 0 else vt[g % 2][:, x, SEQ:T]
                    mm = nc.tensor.transpose(ps[0:NS, n % 8, x * P:(x + 1) * P], src, ident[:, :])
            else:
                kind, b0, step, cnt = mv
                for x in range(cnt):
                    for hp in range(2):
                        tile = qk[:, g, 2 + hp, :] if kind == 0 else vt[g % 2][:, hp, :]
                        bb = b0 + x * step
                        mm = nc.tensor.transpose(ps[:, n % 8, (2 * x + hp) * P:(2 * x + hp + 1) * P], tile[:, bb * P:(bb + 1) * P], ident[:, :])
            mm.then_inc(s_kvt, 1)
            if mv == ("s", 1):
                nc.tensor.drain().then_inc(s_vfree, 1)

        def scores(n):
            g, b = ATT_BLOCKS[n]
            if n >= 2:
                pe.wait_ge(s_max, n - 1)
            w = 2 * P if two_key_blocks(g, b) else P
            k0 = (b + 1) * P - w
            for h in range(NH):
                r = slice(HD * (h % 2), HD * (h % 2) + HD)
                mm = nc.tensor.matmul(ps[:, 2 * (n % 2) + h % 2, (h // 2) * 256:(h // 2) * 256 + w], qk[r, g, h // 2, b * P:(b + 1) * P],
                                      qk[r, g, 2 + h // 2, k0:k0 + w], start=True, stop=True)
            mm.then_inc(s_S, 1)

        def turn_probs(n):
            g, b = ATT_BLOCKS[n]
            pe.wait_ge(s_P, n + 1)
            if n >= 1:
                pe.wait_ge(s_pta, n)
                pe.wait_ge(s_ptd, n)
            two = two_key_blocks(g, b)
            for x in range(2 if two else 1):
                for h in range(NH):
                    to = ps[:, 4 + x, h * P:(h + 1) * P] if two else ps[:, 4 + h // 2, (h % 2) * P:(h % 2 + 1) * P]
                    mm = nc.tensor.transpose(to, pb[:, n % 2, h, x * P:(x + 1) * P], ident[:, :])
            mm.then_inc(s_PT, 1)

        def weighted_sums(n):
            g, b = ATT_BLOCKS[n]
            pe.wait_ge(s_pta, n + 1)
            pe.wait_ge(s_ptd, n + 1)
            if n >= 2:
                pe.wait_ge(s_Oe, n - 1)
            nk = 2 if two_key_blocks(g, b) else 1
            for h in range(NH):
                for x in range(nk):
                    mm = nc.tensor.matmul(ps[:, 6 + n % 2, h * HD:(h + 1) * HD], pt[:, n % 2, x * NH + h, :],
                                          kv[:, g, b + 1 - nk + x, 1, h * HD:(h + 1) * HD], start=x == 0, stop=x == nk - 1)
            mm.then_inc(s_O, 1)

        pe.wait_ge(s_kva, (len(MOVES) + 1) // 2)
        pe.wait_ge(s_kvd, len(MOVES) // 2)
        for n in range(NB + 2):
            if n < NB:
                scores(n)
            if 1 <= n <= NB:
                turn_probs(n - 1)
            if n >= 2:
                weighted_sums(n - 2)

        pe.wait_ge(s_row, 16 * 4 * NG)
        pe.wait_ge(s_Oe, NB)
        for g in range(NG):
            for k in range(2):
                mm = nc.tensor.transpose(ps[0:HD, 2 + g, k * P:(k + 1) * P], rowqk[:, g, k, :], ident[:, :])
        mm.then_inc(s_rowT, 1)
        pe.wait_ge(s_rowt, 1)
        for g in range(NG):
            pe.wait_ge(s_sc, DEC_B * (g + 1))
            nc.tensor.transpose(ps[:, 5 + g, 0:P], sc[:, g, :], ident[:, :])
            nc.tensor.matmul(ps[:, 5 + g, P:2 * P], rowt[0:HD, g, 0, :], rowt[0:HD, g, 1, :], start=True, stop=True).then_inc(s_snew, 1)
        pe.wait_ge(s_pexp, 1)
        for g in range(NG):
            for x in range(2):
                mm = nc.tensor.transpose(ps[:, g, x * P:(x + 1) * P], prow[:, g, x * P:(x + 1) * P], ident[:, :])
        mm.then_inc(s_ppT, 1)
        pe.wait_ge(s_ptr, 1)
        for n in range(NG * DEC_B):
            g, b = n // DEC_B, n % DEC_B
            m = NG * DEC_B + n
            pe.wait_ge(s_kc[m % 4], 16 * (m // 4 + 1))
            for s in range(DEC_S if g else 1):
                w = NH if g else NH * DEC_S
                col = b * NH * DEC_S + s * NH
                for hp in range(2):
                    mm = nc.tensor.matmul(ps[:, 3, hp * P + col:hp * P + col + w], kc[m % 4][:, s, hp * P:(hp + 1) * P], ptr[:, g, 0, col:col + w],
                                          start=n == 0 and hp == 0 and s == 0, stop=False, skip_group_check=True)
            mm.then_inc(s_kcf, 1)
        for g in range(NG):
            for hp in range(2):
                mm = nc.tensor.matmul(ps[:, 3, hp * P:(hp + 1) * P], rowv[:, g, :, :].rearrange("p a d -> p (a d)"), ptr[:, g, 1, :],
                                      start=False, stop=g == NG - 1, skip_group_check=True)
        mm.then_inc(s_pv, 1)
        pe.wait_ge(s_comb, 1)
        for hp in range(2):
            for q in range(2):
                bank = 4 + 2 * hp + q
                for t in range(4):
                    tt = 4 * q + t
                    mm = nc.tensor.transpose(ps[:, bank, t * P:(t + 1) * P], o0[:, tt, hp * P:(hp + 1) * P], ident[:, :])
                mm.then_inc(s_oT, 1)

        pe.wait_ge(s_oTl, 4 + 2)
        for j in range(KT):
            pe.wait_ge(s_lo, ATT0 + j // 4 + 1)
            s = j % 2
            for c in range(NCH):
                if j >= 2:
                    pe.wait_ge(s_zfd[s], NCH * ((Z_ATT0 + j) // 2 - FREED_BY_ACT - 1) + c + 1)
                for k in range(2):
                    w0 = k * 512 + (j % 4) * P
                    mm = split_products(z(s, c), (whi[j // 4][:, w0:w0 + P], wlo[j // 4][:, w0:w0 + P]), k,
                                        othi[:, k, cols(c)], otlo[:, k, cols(c)], k == 0, k == 1)
                mm.then_inc(s_z[s], 1)
        pe.wait_ge(s_slo, KT)
        with pe.Fori(0, KT // 2) as j:
            for s in range(2):
                tile_job(s, 2 * j + (CO0 + s), shi, slo, (s_zfd, NCH * j + (NCH * (Z_CO0 // 2 - FREED_BY_ACT - 1) + 1)))

        def turn_x(j, c):
            r = 3 * j + c
            if r >= 2:
                pe.wait_ge(s_xte, r - 1)
            if c == 0:
                pe.wait_ge(s_xj[j % 2], 32 * (j // 2 + 1))
            for x in range(4 if c < 2 else 1):
                n = P if c < 2 else NS
                mm = nc.tensor.transpose(ps[:, 6 + r % 2, x * P:x * P + n], xj[j % 2][0:n, 4 * c + x, :], ident[0:n, 0:n])
            mm.then_inc(s_xT, 1)

        for c in range(NCH):
            turn_x(0, c)
        pe.wait_ge(s_hlo, NCH * KT)
        for j in range(KT):
            tile_job(j % 2, OUT0 + j, hhi, hlo, (s_zfd, NCH * ((Z_OUT0 + j) // 2 - FREED_BY_ACT - 1) + 1),
                     after=(lambda c, j=j: turn_x(j + 1, c)) if j + 1 < KT else None)
        pe.wait_ge(s_sqs, KT)
        for c in range(NCH):
            if c == 2:
                pe.wait_ge(s_r2s, 1)
            nc.tensor.matmul(ps[:, 6 + c % 2, 0:CH], allmean[:, :], sqs[:, cols(c)], start=True, stop=True).then_inc(s_r2, 1)

        def down(i, n, zn, b, half):
            pe.wait_ge(s_lo, n + 1)
            for j in range(4):
                s = j % 2
                for c in range(NCH):
                    pe.wait_ge(s_zfd[s], NCH * zn + (NCH * (j // 2 - FREED_BY_ACT - 1) + c + 1))
                    for k in range(2):
                        w0 = k * 512 + j * P
                        mm = split_products(z(s, c), (whi[half][:, w0:w0 + P], wlo[half][:, w0:w0 + P]), k,
                                            achi[b][:, k, cols(c)], aclo[b][:, k, cols(c)], k == 0, k == 1)
                    mm.then_inc(s_z[s], 1)

        pe.wait_ge(s_nlo, KT)
        for t in range(4):
            tile_job(t % 2, FFN0 + t, nhi, nlo, (s_zfd, NCH * ((Z_FFN0 + t) // 2 - FREED_BY_ACT - 1) + 1))
        with pe.Fori(0, (NIT - 1) // 2) as ii:
            for e in range(2):
                for t in range(4):
                    tile_job(t % 2, 12 * ii + (FFN0 + 4 + 6 * e + t), nhi, nlo,
                             (s_zfd, 12 * NCH * ii + (NCH * ((Z_FFN0 + 4 + 12 * e + t) // 2 - FREED_BY_ACT - 1) + 1)))
                pe.wait_ge(s_alo2, 4 * NCH * ii + 2 * NCH * (e + 1))
                for half in range(2):
                    down(None, 12 * ii + (FFN0 + 8 + 6 * e + half), 12 * ii + (Z_FFN0 + 8 + 12 * e + 4 * half) // 2, e, half)
        pe.wait_ge(s_alo2, 2 * NCH * NIT)
        for half in range(2):
            down(None, NJOBS - 2 + half, (Z_FFN0 + 12 * NIT - 8 + 4 * half) // 2, 0, half)
        pe.wait_ge(s_fin, 1)
        for t in range(KT + 1):
            n = P if t < KT else NS
            for h in range(2):
                if t >= 4:
                    pe.wait_ge((s_yea, s_yed)[h], t - 3)
                for k in range(4):
                    mm = nc.tensor.transpose(ps[0:n, 2 * (t % 4) + h, k * P:(k + 1) * P], x1[:, 4 * h + k, t * P:t * P + n], ident[:, :])
                mm.then_inc(s_yT, 1)

    @block.scalar
    def _(act):
        def split_hi(slot, n, z2, first=False):
            act.wait_ge(s_raw[slot], 16 * z2 + 16)
            if isinstance(n, int) and n >= 2:
                finished(act, n - 2)
            elif not first:
                act.wait_ge(s_z[slot], NCH * z2)
            nc.scalar.copy(whi[slot][:, :], raw[slot][:, :]).then_inc(s_hi, 1)

        act.wait_ge(s_pad, 1)

        def stats(t):
            n = P if t < KT else NS
            act.wait_ge(s_x[t], 16)
            act.activation(junk[0:n, :], xtok[0:n, t, :], ACT.Square, accum_out=ss[0:n, t:t + 1])
            act.drain()
            act.activation(rs9[0:n, t:t + 1], ss[0:n, t:t + 1], ACT.Sqrt, bias=eps[0:n, 0:1], scale=1.0 / D).then_inc(s_rs, 1)

        def evac(t):
            n = P if t < KT else NS
            for h in range(2):
                act.wait_ge(s_tr, 2 * t + h + 1)
                act.copy(xhi[:, 4 * h:4 * h + 4, t * P:t * P + n],
                         ps[:, (2 * t + h) % 4, 0:4 * n].rearrange("p (k n) -> p k n", k=4)).then_inc(s_ahi, 1)

        for t in range(KT + 2):
            if t <= KT:
                stats(t)
            if t == 1:
                split_hi(0, 0, 0, first=True)
                split_hi(1, 1, 0, first=True)
            if t >= 1:
                evac(t - 1)
        def glu_sigmoid(j, first=False):
            split_hi(0, 2 * j + 2, j + 1)
            for c in range(NCH):
                act.wait_ge(s_z[1], NCH * j + (c + 1))
                if not first:
                    act.wait_ge(s_zfd[0], NCH * j + (c + 1 - NCH))
                act.activation(sg[:, cols(c)], z(1, c), ACT.Sigmoid).then_inc(s_sig, 1)
            split_hi(1, 2 * j + 3, j + 1)

        glu_sigmoid(0, first=True)
        with act.Fori(1, KT) as j:
            glu_sigmoid(j)
        for g in range(NG):
            for i in range(6):
                m = QKV0 + 6 * g + i
                s = m % 2
                for c in range(NCH):
                    if 1 <= i <= 4:
                        q = 12 * g + NCH * (i - 1) + c
                        act.wait_ge(s_ssr, q + 1)
                        if i > 1:
                            act.wait_ge(s_ztd, NCH * (m - 2 - QKV0) + c + 1)
                        act.activation(rsb[:, cols(c)], ps[:, 6 + q % 2, 0:CH], ACT.Sqrt, bias=eps[:, 0:1]).then_inc(s_sqrt, 1)
                    act.wait_ge(s_z[s], NCH * (m // 2) + c + 1)
                    if i < 4:
                        act.activation(sqb[:, cols(c)], z(s, c), ACT.Square).then_inc(s_sq, 1)
                split_hi(s, m + 2, m // 2 + 1)
        for j in range(KT):
            for s in range(2):
                m = GATE0 + 2 * j + s
                split_hi(s, m + 2, m // 2 + 1)
                for c in range(NCH):
                    act.wait_ge(s_z[s], NCH * (m // 2) + c + 1)
                    act.wait_ge(s_zst[s], 16 * ((m - QKV0) // 2))
                    act.activation(zt[s][:, cols(c)], z(s, c), ACT.Sigmoid).then_inc(s_zta, 1)
                    act.drain().then_inc(s_zfa[s], 1)

        act.wait_ge(s_ut, 1)
        act.copy(urow[:, :].rearrange("p (a b) -> p a b", a=2), ps[0:HIST, 0:2, :]).then_inc(s_urow, 1)
        act.wait_ge(s_ut, 2)
        act.copy(urows[:, :].rearrange("p (a b) -> p a b", a=2), ps[0:NS, 2:4, :]).then_inc(s_urow, 1)
        for i in range(2):
            act.wait_ge(s_zst[i], 16 * (ATT0 - QKV0) // 2)
        for k in range(KT):
            act.wait_ge(s_ln["cen"], k + 1)
            if k >= 2:
                act.wait_ge(s_ln["var"], k - 1)
            act.activation(lsq[:, k % 2, :], conv[:, k, :], ACT.Square).then_inc(s_ln["sq"], 1)
        act.wait_ge(s_ln["var"], KT)
        for c in range(NCH):
            act.activation(lrs[:, cols(c)], ps[:, 4 + c, 0:CH], ACT.Sqrt, bias=eps[:, 1:2]).then_inc(s_ln["root"], 1)
        for k in range(KT):
            act.wait_ge(s_ln["norm"], k + 1)
            act.activation(conv[:, k, :], conv[:, k, :], ACT.Silu, bias=vec[:, k, V_LB:V_LB + 1], scale=vec[:, k, V_LW:V_LW + 1]).then_inc(s_ln["act"], 1)

        def move_out(eng, n, sem_):
            g, mv = MOVES[n]
            eng.wait_ge(s_kvt, n + 1)
            if mv[0] == "s":
                w = 4 if mv[1] == 0 else 2
                dst = srows[0:NS, g, 0:2, :] if mv[1] == 0 else srows[0:NS, g, 2, :]
                src = ps[0:NS, n % 8, 0:w * P]
                if mv[1] == 0:
                    src = src.rearrange("p (k d) -> p k d", k=2)
            else:
                kind, b0, step, cnt = mv
                dst = kv[:, g, b0:b0 + (cnt - 1) * step + 1:step, kind, :] if cnt > 1 else kv[:, g, b0:b0 + 1, kind, :]
                src = ps[:, n % 8, 0:cnt * 2 * P].rearrange("p (b d) -> p b d", b=cnt)
            (eng.copy if eng is act else nc.vector.tensor_copy)(dst, src).then_inc(sem_, 1)

        move_rows.append(move_out)
        act.wait_ge(s_ln["norm"], KT)
        for n in range(0, len(MOVES), 2):
            move_out(act, n, s_kva)

        def exps(n):
            g, b = ATT_BLOCKS[n]
            act.wait_ge(s_max, n + 1)
            w = 2 * P if two_key_blocks(g, b) else P
            row = o0[:, b, :] if g == 0 else ob[:, n % 4, :]
            for h in range(NH):
                last = act.activation(pb[:, n % 2, h, 0:w], pb[:, n % 2, h, 0:w], ACT.Exp, bias=nmx[:, n % 2, h:h + 1], scale=SCALE,
                                      accum_out=row[:, GW + NH + h:GW + NH + h + 1])
            last.then_inc(s_P, 1)

        def probs_out(n):
            g, b = ATT_BLOCKS[n]
            act.wait_ge(s_PT, n + 1)
            if n >= 2:
                act.wait_ge(s_O, n - 1)
            if two_key_blocks(g, b):
                act.copy(pt[:, n % 2, NH:2 * NH, :], ps[:, 5, :].rearrange("p (h q) -> p h q", h=NH)).then_inc(s_pta, 1)
            else:
                act.copy(pt[:, n % 2, 2:NH, :], ps[:, 5, 0:2 * P].rearrange("p (h q) -> p h q", h=2)).then_inc(s_pta, 1)

        def outputs(n):
            g, b = ATT_BLOCKS[n]
            act.wait_ge(s_O, n + 1)
            row = o0[:, b, :] if g == 0 else ob[:, n % 4, :]
            act.copy(row[:, 0:GW], ps[:, 6 + n % 2, 0:GW]).then_inc(s_Oe, 1)

        for n in range(NB + 2):
            if n < NB:
                exps(n)
            if 1 <= n <= NB:
                probs_out(n - 1)
            if n >= 2:
                outputs(n - 2)
        act.wait_ge(s_rowT, 1)
        act.copy(rowt[0:HD, :, :, :].rearrange("p g k r -> p g (k r)"), ps[0:HD, 2:5, 0:2 * P]).then_inc(s_rowt, 1)
        act.wait_ge(s_prow, 1)
        act.activation(prow[:, :, :], prow[:, :, :], ACT.Exp, bias=sst[:, 1:2], scale=SCALE, accum_out=sst[:, 2:3]).then_inc(s_pexp0, 1)
        act.wait_ge(s_ppT, 1)
        act.copy(ptr[:, :, :, :].rearrange("p g k r -> p g (k r)"), ps[:, 0:NG, 0:2 * P]).then_inc(s_ptr, 1)
        act.wait_ge(s_cd, 1)
        for g in range(NG):
            last = act.activation(cw[g + 1][:, :, :], cw[g + 1][:, :, :], ACT.Exp, scale=SCALE)
        last.then_inc(s_cw, 1)
        act.wait_ge(s_pv, 1)
        for h in range(NH):
            r = slice(HD * (h % 2), HD * (h % 2) + HD)
            src = ps[r, 3, (h // 2) * P:(h // 2 + 1) * P].rearrange("p (x h) -> p x h", h=NH)[:, :, h]
            last = act.copy(othi[r, h // 2, SEQ:T], src)
        last.then_inc(s_oTh, 1)
        for x in range(4):
            act.wait_ge(s_oT, x + 1)
            act.copy(othi[:, x // 2, (x % 2) * 512:(x % 2) * 512 + 512], ps[:, 4 + x, :]).then_inc(s_oTh, 1)
        for k in range(KT):
            act.copy(shi[:, k, :], conv[:, k, :]).then_inc(s_shi, 1)
        split_hi(0, CO0, CO0 // 2)
        split_hi(1, CO0 + 1, CO0 // 2)

        for j in range(KT):
            for c in range(NCH):
                act.wait_ge(s_ht, NCH * j + c + 1)
                act.copy(hhi[:, j, cols(c)], ht[j % 2][:, cols(c)]).then_inc(s_hhi, 1)
            split_hi(j % 2, CO0 + j + 2, (CO0 + j + 2) // 2)
        def x_out(j, c):
            r = 3 * j + c
            act.wait_ge(s_xT, r + 1)
            if j >= 1:
                act.wait_ge(s_x1, NCH * j)
            n = 512 if c < 2 else NS
            act.copy(xtj[:, c * 512:c * 512 + n], ps[:, 6 + r % 2, 0:n]).then_inc(s_xte, 1)

        for j in range(KT):
            for c in range(NCH):
                x_out(j, c)
            split_hi(j % 2, OUT0 + j + 2, (OUT0 + j + 2) // 2)
            act.wait_ge(s_x1, NCH * (j + 1))
            if j >= 1:
                act.wait_ge(s_sqs, j)
            act.activation(sqj[:, :], x1[:, j, :], ACT.Square).then_inc(s_sqj, 1)
        for c in range(NCH):
            act.wait_ge(s_r2, c + 1)
            act.activation(sqs[:, cols(c)], ps[:, 6 + c % 2, 0:CH], ACT.Sqrt, bias=eps[:, 0:1]).then_inc(s_r2s, 1)
        for k in range(KT):
            act.wait_ge(s_n, k + 1)
            act.copy(nhi[:, k, :], ht[k % 2][:, :]).then_inc(s_nhi, 1)

        def ffn_up(e, n0, cc, after_first=True):
            for t in range(2):
                for c in range(NCH):
                    act.wait_ge(s_z[0], cc["z0"] + (NCH * t + c + 1))
                    if after_first:
                        act.wait_ge(s_alo2, cc["q"] + (NCH * (t - 2) + c + 1))
                    act.activation(sil[t][:, cols(c)], z(0, c), ACT.Silu).then_inc(s_sil, 1)
                split_at(0, n0 + 2 * t + 2, cc["r"] + (t + 1), cc["z0"] + NCH * (t + 1), 0)
                for c in range(NCH):
                    act.wait_ge(s_gt, cc["q"] + (NCH * t + c + 1))
                    act.copy(achi[e][:, t, cols(c)], sil[t][:, cols(c)]).then_inc(s_ahi2, 1)
                split_at(1, n0 + 2 * t + 3, cc["r"] + (t + 1), cc["z0"] + NCH * (t + 1), 1)

        def split_at(slot, n, r, zc, zs):
            act.wait_ge(s_raw[slot], 16 * r + 16)
            act.wait_ge(s_z[zs], zc)
            nc.scalar.copy(whi[slot][:, :], raw[slot][:, :]).then_inc(s_hi, 1)

        ffn_up(0, FFN0, {"z0": NCH * (Z_FFN0 // 2), "q": 0, "r": FFN0 // 2}, after_first=False)
        with act.Fori(0, (NIT - 1) // 2) as ii:
            for e in range(2):
                base_n = FFN0 + 4 + 6 * e
                zb = 12 * NCH * ii
                z0 = NCH * ((Z_FFN0 + 4 + 12 * e) // 2)
                ffn_up(1 - e, 12 * ii + base_n, {"z0": zb + z0, "q": 4 * NCH * ii + 2 * NCH * (e + 1), "r": 6 * ii + base_n // 2})
                for half in range(2):
                    split_at(half, 12 * ii + (base_n + 6 + half), 6 * ii + (base_n // 2 + 3), zb + (z0 + NCH * (4 + 2 * half)), 1)
        for t in range(KT + 1):
            n = P if t < KT else NS
            act.wait_ge(s_yT, 2 * t + 1)
            if t >= 4:
                act.wait_ge(s_yst[t % 4], 16 * (t // 4))
            act.copy(ytok[t % 4][0:n, 0:512], ps[0:n, 2 * (t % 4), :]).then_inc(s_yea, 1)

    @block.vector
    def _(dve):
        V = nc.vector

        def split_lo(slot, n, z2):
            dve.wait_ge(s_hi, n + 1)
            V.tensor_tensor(wlo[slot][:, :], raw[slot][:, :], whi[slot][:, :].bitcast(F32), ALU.subtract).then_inc(s_lo, 1)

        V.memset(eps[:, 0:1], RMS_EPS)
        V.memset(eps[:, 1:2], LN_EPS)
        V.memset(u[:, :, 0:HIST], 0.0).then_inc(s_pad, 1)
        dve.wait_ge(s_const, 16 * NC0)

        def scale(t):
            n = P if t < KT else NS
            dve.wait_ge(s_rs, t + 1)
            V.reciprocal(rs9[0:n, t:t + 1], rs9[0:n, t:t + 1])
            dve.drain()
            V.scalar_tensor_tensor(xtok[0:n, t, :], xtok[0:n, t, :], rs9[0:n, t:t + 1], wb[0:n, :], ALU.mult, ALU.mult).then_inc(s_xs, 1)

        def evac(t):
            n = P if t < KT else NS
            for h in range(2):
                dve.wait_ge(s_ahi, 2 * t + h + 1)
                dst = slice(t * P, t * P + n)
                V.tensor_tensor(xlo[:, 4 * h:4 * h + 4, dst], ps[:, (2 * t + h) % 4, 0:4 * n].rearrange("p (k n) -> p k n", k=4),
                                xhi[:, 4 * h:4 * h + 4, dst].bitcast(F32), ALU.subtract).then_inc(s_alo, 1)

        for t in range(KT + 2):
            if t <= KT:
                scale(t)
            if t == 2:
                split_lo(0, 0, 0)
                split_lo(1, 1, 0)
            if t >= 1:
                evac(t - 1)
        dve.wait_ge(s_vt, 1)
        V.tensor_copy(vec[:, :, :], ps[:, 4, 0:KT * NVEC].rearrange("p (k v) -> p k v", k=KT)).then_inc(s_vec, 1)
        for k in range(KT):
            dve.wait_ge(s_stt, k + 1)
            V.tensor_copy(u[:, k, HIST + SEQ:].rearrange("p (b r) -> p b r", b=DEC_B)[:, :, 0:HIST],
                          ps[:, 5 + k % 2, 0:DEC_B * HIST].rearrange("p (b r) -> p b r", b=DEC_B)).then_inc(s_stu, 1)

        def tap(k, tau):
            dve.drain()
            dst, src, w = conv[:, k, 0:SEQ], u[:, k, tau:tau + SEQ], vec[:, k, tau:tau + 1]
            if tau == 0:
                return V.tensor_scalar(dst, src, w, vec[:, k, V_B:V_B + 1], ALU.mult, ALU.add)
            return V.scalar_tensor_tensor(dst, src, w, dst, ALU.mult, ALU.add)

        for j in range(KT):
            split_lo(0, 2 * j + 2, j + 1)
            for c in range(NCH):
                dve.wait_ge(s_sig, NCH * j + c + 1)
                dve.wait_ge(s_z[0], NCH * j + c + 1)
                n = CH if c < 2 else PC2
                last = V.tensor_tensor(u[:, j, HIST + c * CH:HIST + c * CH + n], z(0, c)[:, 0:n], sg[:, c * CH:c * CH + n], ALU.mult)
                if c == 2:
                    last = V.tensor_tensor(u[:, j, HIST + SEQ:].rearrange("p (b r) -> p b r", b=DEC_B)[:, :, HIST:SEG],
                                           z(0, c)[:, n:CH].rearrange("p (b s) -> p b s", b=DEC_B),
                                           sg[:, SEQ:T].rearrange("p (b s) -> p b s", b=DEC_B), ALU.mult)
                last.then_inc(s_zfd[0], 1)
                dve.drain().then_inc(s_zfd[1], 1)
            split_lo(1, 2 * j + 3, j + 1)
            for tau in range(TAPS_GLU):
                tap(j, tau)
        def qkv_out(m, c):
            g, i, s = (m - QKV0) // 6, (m - QKV0) % 6, m % 2
            if i < 4:
                dve.wait_ge(s_sqrt, 12 * g + NCH * i + c + 1)
                V.reciprocal(rsb[:, cols(c)], rsb[:, cols(c)])
                dve.drain()
            if m - QKV0 >= 2:
                dve.wait_ge(s_zst[s], 16 * ((m - QKV0) // 2))
            dve.wait_ge(s_z[s], NCH * (m // 2) + c + 1)
            for (dst, src), (_, r) in zip(permuted(g, zt[s], z(s, c), c), permuted(g, zt[s], rsb[:, cols(c)], c)):
                if i < 4:
                    last = V.scalar_tensor_tensor(dst, src, qkw[:, i // 2:i // 2 + 1], r, ALU.mult, ALU.mult)
                else:
                    last = V.tensor_copy(dst, src)
            last.then_inc(s_ztd, 1)
            dve.drain().then_inc(s_zfd[s], 1)

        for g in range(NG):
            for i in range(6):
                m = QKV0 + 6 * g + i
                for c in range(NCH):
                    if m > QKV0:
                        qkv_out(m - 1, c)
                    for v in range(4 * i + (0, 1, 2)[c], 4 * i + (1, 2, 4)[c]):
                        tap(v % KT, TAPS_GLU + 3 * g + v // KT)
                split_lo(m % 2, m + 2, m // 2 + 1)
        for c in range(NCH):
            qkv_out(GATE0 - 1, c)
        for j in range(KT):
            for s in range(2):
                m = GATE0 + 2 * j + s
                split_lo(s, m + 2, m // 2 + 1)
                if s == 0:
                    for tau in range(TAPS_GLU + TAPS_QKV, TAPS_GLU + TAPS_QKV + 5):
                        tap(j, tau)
                else:
                    for tau in range(TAPS_GLU + TAPS_QKV + 5, CW):
                        tap(j, tau)
                    us = u[:, j, HIST + SEQ:].rearrange("p (b r) -> p b r", b=DEC_B)
                    win = bass.AP(us.tensor, us.offset, [us.ap[0], [SEG, DEC_B], [1, DEC_S], [1, CW]])
                    wv = vec[:, j, 0:CW]
                    wr = bass.AP(wv.tensor, wv.offset, [wv.ap[0], [0, DEC_B], [0, DEC_S], [1, CW]])
                    V.tensor_tensor(sprod[:, :, :, :], win, wr, ALU.mult)
                    dve.drain()
                    V.tensor_reduce(conv[:, j, SEQ:T], sprod[:, :, :, :].rearrange("p b s w -> p (b s) w"), AX_X, ALU.add)
                    dve.drain()
                    V.tensor_scalar(conv[:, j, SEQ:T], conv[:, j, SEQ:T], vec[:, j, V_B:V_B + 1], None, ALU.add)
        dve.drain().then_inc(s_conv, 1)
        V.tensor_copy(utail[:, :, :].rearrange("p k (b s) -> p k b s", b=DEC_B),
                      u[:, :, HIST + SEQ:].rearrange("p k (b r) -> p k b r", b=DEC_B)[:, :, :, HIST:SEG]).then_inc(s_utail, 1)
        dve.wait_ge(s_ln["mean"], NCH)
        for k in range(KT):
            for c in range(NCH):
                last = V.tensor_tensor(conv[:, k, cols(c)], conv[:, k, cols(c)], ps[:, 4 + c, 0:CH], ALU.subtract)
            last.then_inc(s_ln["cen"], 1)
        dve.wait_ge(s_ln["root"], NCH)
        V.reciprocal(lrs[:, :], lrs[:, :])
        dve.drain()
        for k in range(KT):
            V.tensor_tensor(conv[:, k, :], conv[:, k, :], lrs[:, :], ALU.mult).then_inc(s_ln["norm"], 1)
        dve.drain()
        for n in range(1, len(MOVES), 2):
            move_rows[0](dve, n, s_kvd)

        def maxima(n):
            g, b = ATT_BLOCKS[n]
            dve.wait_ge(s_S, n + 1)
            if n >= 2:
                dve.wait_ge(s_PT, n - 1)
            if n == 0:
                dve.wait_ge(s_srows, 16 * NG)
                dve.wait_ge(s_out, 16 * NOUT_C)
            if n >= 12:
                dve.wait_ge(s_ost[n % 4], 16 * ((n - 8) // 4) if n < 20 else 32 + 32 * ((n - 16) // 4))
            w = 2 * P if two_key_blocks(g, b) else P
            mask = (band[:, :] if w == 2 * P else band[:, P:2 * P]) if g < 2 else pair[:, :]
            row = o0[:, b, :] if g == 0 else ob[:, n % 4, :]
            for h in range(NH):
                V.tensor_tensor_reduce(pb[:, n % 2, h, 0:w], ps[:, 2 * (n % 2) + h % 2, (h // 2) * 256:(h // 2) * 256 + w], mask, 1.0, -3e38,
                                       ALU.add, ALU.max, row[:, GW + h:GW + h + 1])
            dve.drain()
            V.tensor_scalar(nmx[:, n % 2, :], row[:, GW:GW + NH], -SCALE, None, ALU.mult).then_inc(s_max, 1)

        def probs_in(n):
            g, b = ATT_BLOCKS[n]
            dve.wait_ge(s_PT, n + 1)
            if n >= 2:
                dve.wait_ge(s_O, n - 1)
            w = NH if two_key_blocks(g, b) else 2
            V.tensor_copy(pt[:, n % 2, 0:w, :], ps[:, 4, 0:w * P].rearrange("p (h q) -> p h q", h=w)).then_inc(s_ptd, 1)

        for n in range(NB + 1):
            if n < NB:
                maxima(n)
            if n >= 1:
                probs_in(n - 1)
        for n in range(NG * DEC_B):
            g, b = n // DEC_B, n % DEC_B
            dve.wait_ge(s_kc[n % 4], 16 * (n // 4 + 1))
            dve.wait_ge(s_qb[n % 2], 16 * (n // 2 + 1))
            keys = kc[n % 4][:, :, :] if g else kc[n % 4][:, 0:1, :].to_broadcast([P, DEC_S, GW])
            V.tensor_tensor(prod[n % 2][:, :, :], keys, qb[n % 2][:, :, :], ALU.mult).then_inc(s_prod, 1)
            dve.drain()
            V.tensor_reduce(sc[:, g, b * 16:(b + 1) * 16], prod[n % 2][:, :, :].rearrange("p s (h d) -> p (s h) d", h=NH), AX_X, ALU.add).then_inc(s_sc, 1)
        dve.wait_ge(s_snew, NG)
        V.tensor_tensor(prow[:, :, :], ps[:, 5:5 + NG, 0:2 * P], smask[:, :, :], ALU.add)
        dve.drain()
        V.tensor_reduce(sst[:, 0:1], prow[:, :, :].rearrange("p g k -> p (g k)"), AX_X, ALU.max)
        dve.drain()
        V.tensor_scalar(sst[:, 1:2], sst[:, 0:1], -SCALE, None, ALU.mult).then_inc(s_prow, 1)
        dve.wait_ge(s_pexp0, 1)
        V.reciprocal(sst[:, 3:4], sst[:, 2:3])
        dve.drain()
        V.tensor_scalar(prow[:, :, :], prow[:, :, :], sst[:, 3:4], None, ALU.mult).then_inc(s_pexp, 1)
        dve.wait_ge(s_o12, 32)
        dve.wait_ge(s_pv, 1)
        rows = [o0[:, :, :], o12[:, 0], o12[:, 1]]
        mx = [r[:, :, GW:GW + NH] for r in rows]
        V.tensor_tensor(cw[0][:, :, :], mx[0], mx[1], ALU.max)
        dve.drain()
        V.tensor_tensor(cw[0][:, :, :], cw[0][:, :, :], mx[2], ALU.max)
        dve.drain()
        for g in range(NG):
            last = V.tensor_tensor(cw[g + 1][:, :, :], mx[g], cw[0][:, :, :], ALU.subtract)
        last.then_inc(s_cd, 1)
        dve.wait_ge(s_cw, 1)
        for g in range(NG):
            V.tensor_tensor(cw[g + 4][:, :, :], cw[g + 1][:, :, :], rows[g][:, :, GW + NH:SW], ALU.mult)
        dve.drain()
        V.tensor_tensor(cw[4][:, :, :], cw[4][:, :, :], cw[5][:, :, :], ALU.add)
        dve.drain()
        V.tensor_tensor(cw[4][:, :, :], cw[4][:, :, :], cw[6][:, :, :], ALU.add)
        dve.drain()
        V.reciprocal(cw[7][:, :, :], cw[4][:, :, :])
        dve.drain()
        for g in range(NG):
            V.tensor_tensor(cw[g + 1][:, :, :], cw[g + 1][:, :, :], cw[7][:, :, :], ALU.mult)
        dve.drain()

        def by_head(x):
            return x.rearrange("p t (h d) -> p t h d", h=NH)

        for g in range(NG):
            for h in range(NH):
                f = cw[g + 1][:, :, h:h + 1].to_broadcast([P, KT, HD])
                src = rows[g][:, :, h * HD:(h + 1) * HD]
                V.tensor_tensor(src, src, f, ALU.mult)
        dve.drain()
        V.tensor_tensor(o0[:, :, 0:GW], o0[:, :, 0:GW], o12[:, 0, :, 0:GW], ALU.add)
        dve.drain()
        V.tensor_tensor(o0[:, :, 0:GW], o0[:, :, 0:GW], o12[:, 1, :, 0:GW], ALU.add).then_inc(s_comb, 1)
        dve.wait_ge(s_oTh, 1)
        for h in range(NH):
            r = slice(HD * (h % 2), HD * (h % 2) + HD)
            src = ps[r, 3, (h // 2) * P:(h // 2 + 1) * P].rearrange("p (x h) -> p x h", h=NH)[:, :, h]
            last = V.tensor_tensor(otlo[r, h // 2, SEQ:T], src, othi[r, h // 2, SEQ:T].bitcast(F32), ALU.subtract)
        last.then_inc(s_oTl, 1)
        for x in range(4):
            dve.wait_ge(s_oTh, x + 2)
            cc = slice((x % 2) * 512, (x % 2) * 512 + 512)
            V.tensor_tensor(otlo[:, x // 2, cc], ps[:, 4 + x, :], othi[:, x // 2, cc].bitcast(F32), ALU.subtract).then_inc(s_oTl, 1)
        dve.drain().then_inc(s_oTl, 1)

        def gated_a(j):
            for c in range(NCH):
                dve.wait_ge(s_sgs[j % 2], 16 * (j // 2 + 1))
                dve.wait_ge(s_z[j % 2], NCH * ((Z_ATT0 + j) // 2) + c + 1)
                V.tensor_tensor(ha[:, j, cols(c)], z(j % 2, c), sgs[j % 2][:, cols(c)], ALU.mult).then_inc(s_zfd[j % 2], 1)

        for k in range(KT):
            if k < 2:
                gated_a(k)
            dve.wait_ge(s_shi, k + 1)
            V.tensor_tensor(slo[:, k, :], conv[:, k, :], shi[:, k, :].bitcast(F32), ALU.subtract).then_inc(s_slo, 1)
            if k >= 2:
                gated_a(k)
        split_lo(0, CO0, 0)
        split_lo(1, CO0 + 1, 0)
        for j in range(KT):
            s = j % 2
            for c in range(NCH):
                dve.wait_ge(s_sgs[s], 16 * ((KT + j) // 2 + 1))
                dve.wait_ge(s_z[s], NCH * ((Z_CO0 + j) // 2) + c + 1)
                V.tensor_tensor(ht[s][:, cols(c)], z(s, c), sgs[s][:, cols(c)], ALU.mult).then_inc(s_zfd[s], 1)
                dve.drain()
                V.tensor_tensor(ht[s][:, cols(c)], ht[s][:, cols(c)], ha[:, j, cols(c)], ALU.add).then_inc(s_ht, 1)
                dve.wait_ge(s_hhi, NCH * j + c + 1)
                V.tensor_tensor(hlo[:, j, cols(c)], ht[s][:, cols(c)], hhi[:, j, cols(c)].bitcast(F32), ALU.subtract).then_inc(s_hlo, 1)
            split_lo(s, CO0 + j + 2, 0)
        for j in range(KT):
            s = j % 2
            dve.wait_ge(s_xte, NCH * (j + 1))
            for c in range(NCH):
                dve.wait_ge(s_z[s], NCH * ((Z_OUT0 + j) // 2) + c + 1)
                V.tensor_tensor(x1[:, j, cols(c)], z(s, c), xtj[:, cols(c)], ALU.add).then_inc(s_x1, 1)
                dve.drain().then_inc(s_zfd[s], 1)
            split_lo(s, OUT0 + j + 2, 0)
            dve.wait_ge(s_sqj, j + 1)
            if j == 0:
                V.tensor_copy(sqs[:, :], sqj[:, :]).then_inc(s_sqs, 1)
            else:
                V.tensor_tensor(sqs[:, :], sqs[:, :], sqj[:, :], ALU.add).then_inc(s_sqs, 1)
            dve.drain()
        dve.wait_ge(s_r2s, NCH)
        V.reciprocal(sqs[:, :], sqs[:, :])
        dve.drain()
        for k in range(KT + 1):
            if k < KT:
                if k >= 2:
                    dve.wait_ge(s_nhi, k - 1)
                V.scalar_tensor_tensor(ht[k % 2][:, :], x1[:, k, :], vec[:, k, V_NF:V_NF + 1], sqs[:, :], ALU.mult, ALU.mult).then_inc(s_n, 1)
            if k >= 1:
                dve.wait_ge(s_nhi, k)
                V.tensor_tensor(nlo[:, k - 1, :], ht[(k - 1) % 2][:, :], nhi[:, k - 1, :].bitcast(F32), ALU.subtract).then_inc(s_nlo, 1)
            dve.drain()

        def ffn_up(e, n0, cc):
            for t in range(2):
                split_lo(0, n0 + 2 * t + 2, 0)
                for c in range(NCH):
                    dve.wait_ge(s_sil, cc["q"] + (NCH * t + c + 1))
                    dve.wait_ge(s_z[1], cc["z0"] + (NCH * t + c + 1))
                    V.tensor_tensor(sil[t][:, cols(c)], z(1, c), sil[t][:, cols(c)], ALU.mult).then_inc(s_gt, 1)
                    dve.drain().then_inc(s_zfd[0], 1)
                    dve.drain().then_inc(s_zfd[1], 1)
                    dve.wait_ge(s_ahi2, cc["q"] + (NCH * t + c + 1))
                    V.tensor_tensor(aclo[e][:, t, cols(c)], sil[t][:, cols(c)], achi[e][:, t, cols(c)].bitcast(F32), ALU.subtract).then_inc(s_alo2, 1)
                split_lo(1, n0 + 2 * t + 3, 0)

        def ffn_down(half, z0):
            for j in range(4):
                s = j % 2
                for c in range(NCH):
                    dve.wait_ge(s_z[s], z0 + (NCH * (j // 2) + c + 1))
                    V.tensor_tensor(x1[:, 4 * half + j, cols(c)], x1[:, 4 * half + j, cols(c)], z(s, c), ALU.add).then_inc(s_zfd[s], 1)

        ffn_up(0, FFN0, {"z0": NCH * (Z_FFN0 // 2), "q": 0})
        with dve.Fori(0, (NIT - 1) // 2) as ii:
            for e in range(2):
                base_n = FFN0 + 4 + 6 * e
                zb = 12 * NCH * ii
                z0 = NCH * ((Z_FFN0 + 4 + 12 * e) // 2)
                ffn_up(1 - e, 12 * ii + base_n, {"z0": zb + z0, "q": 4 * NCH * ii + 2 * NCH * (e + 1)})
                for half in range(2):
                    ffn_down(half, zb + (z0 + NCH * (2 + 2 * half)))
                    split_lo(half, 12 * ii + (base_n + 6 + half), 0)
                dve.drain()
        for half in range(2):
            ffn_down(half, NCH * ((Z_FFN0 + 12 * NIT - 8) // 2 + 2 * half))
        dve.drain().then_inc(s_fin, 1)
        for t in range(KT + 1):
            n = P if t < KT else NS
            dve.wait_ge(s_yT, 2 * t + 2)
            if t >= 4:
                dve.wait_ge(s_yst[t % 4], 16 * (t // 4))
            V.tensor_copy(ytok[t % 4][0:n, 512:1024], ps[0:n, 2 * (t % 4) + 1, :]).then_inc(s_yed, 1)
    ctx.close()


INPUTS = ["x_prompt", "x_sample", "cache_kv_w128", "cache_kv_w512", "cache_kv_w2048", "state_conv", "norm_mix_w", "w_in",
          "q_norm_w", "k_norm_w", "w_att", "conv_w", "conv_b", "conv_ln_w", "conv_ln_b", "w_conv_out", "w_out",
          "norm_ffn_w", "w_gate_up", "w_down"]

OUTS = [("y_prompt", (1, SEQ, D)), ("y_sample", (DEC_B, DEC_S, D))]
for _g in range(NG):
    OUTS.append((f"kv_prompt{_g}", (1, 1, min(WIN[_g], SEQ), 2, NH, HD)))
    OUTS.append((f"kv_sample{_g}", (1, DEC_B, WIN[_g], 2, NH, HD)))
OUTS += [("conv_prompt", (1, 1, HIST, D)), ("conv_sample", (1, DEC_B, HIST, D))]


def constants():
    import numpy as np
    r = np.arange(P)
    head = (r[:, None] // HD == r[None, :] // HD)
    prev = np.where(r[None, :] >= r[:, None], 0.0, NEG)
    cur = np.where(r[None, :] <= r[:, None], 0.0, NEG)
    s = (r // NH) % DEC_S
    same_seq = (r[:, None] // (NH * DEC_S) == r[None, :] // (NH * DEC_S)) & (r[:, None] % NH == r[None, :] % NH)
    smask = np.zeros((P, NG, 2 * P))
    smask[:, 0, :P] = np.where(r[None, :] >= s[:, None], 0.0, NEG)
    smask[:, 0, P:] = np.where(same_seq & (s[None, :] <= s[:, None]), 0.0, NEG)
    smask[:, 1:, P:] = np.where(np.eye(P) > 0, 0.0, NEG)[:, None, :]
    out = {"c_ident": np.eye(P), "c_headmean": head / HD, "c_allmean": np.full((P, P), 1.0 / D),
           "c_band": np.concatenate([prev, cur], 1), "c_pair": np.where(head & (cur == 0), 0.0, NEG), "c_smask": smask}
    return {k: v.astype(np.float32) for k, v in out.items()}


def kernel(**inputs):
    import numpy as np
    import concourse.bacc as bacc
    from concourse.bass_utils import run_bass_kernel_spmd

    nc = bacc.Bacc("TRN2", target_bir_lowering=False, num_devices=1)
    arrays, a = {}, {}
    given = {n: np.ascontiguousarray(inputs[n]) for n in INPUTS}
    given.update(constants())
    for n, v in given.items():
        arrays[n] = v
        a[n] = nc.dram_tensor(n, v.shape, mybir.dt.from_np(v.dtype), kind="ExternalInput").ap()
    a["scr_z"] = nc.dram_tensor("scr_z", (ATT0 - QKV0, P, T), F32, kind="Internal").ap()
    a["scr_q"] = nc.dram_tensor("scr_q", (NG, 3, NS, GW), F32, kind="Internal").ap()
    a["scr_o"] = nc.dram_tensor("scr_o", (2, SEQ, SW), F32, kind="Internal").ap()
    for n, shape in OUTS:
        a[n] = nc.dram_tensor(n, shape, F32, kind="ExternalOutput").ap()
    build(nc, a)
    r = run_bass_kernel_spmd(nc, [arrays], core_ids=[0])
    return tuple(r.results[0][n] for n, _ in OUTS)
```
